# Optimizing a Trainium2 kernel written in Bass

```python
import jax, jax.numpy as jnp
from jax import lax
import numpy as np

D_MODEL = 1024
BATCH = 1
SEQ = 1024
DEPTH = 1

D_MIX = D_MODEL
D_REC = D_MIX // 2
N_REC_BLOCKS = 8
REC_BLOCK = D_REC // N_REC_BLOCKS
CONV_WIDTH = 4
RGLRU_C = 8.0
D_ATT = D_MIX - D_REC
HEAD_DIM = 64
N_HEADS = D_ATT // HEAD_DIM
Q_BLOCK = 128
D_IN_PROJ = 2 * D_REC + 3 * D_ATT + N_HEADS
N_EXPERTS = 32
TOP_K = 4
D_EXPERT = D_MODEL
SWIGLU_LIMIT = 7.0
SWIGLU_ALPHA = 1.702
EXPERT_BLOCK = 128
EPS = 1e-6

kernel_name = "hybrid_rglru_fox_moe_layer"

def _rmsnorm(x, w):
    xf = x.astype(jnp.float32)
    y = xf * lax.rsqrt(jnp.mean(xf * xf, axis=-1, keepdims=True) + EPS)
    return (y * w.astype(jnp.float32)).astype(x.dtype)

def _rg_lru_group(u, gate, conv_w, conv_b, w_a, b_a, w_i, b_i, lam):
    B, S, _ = u.shape
    f32 = jnp.float32
    up = jnp.pad(u, ((0, 0), (CONV_WIDTH - 1, 0), (0, 0)))
    xc = conv_b + up[:, 0:S] * conv_w[0]
    for tap in range(1, CONV_WIDTH):
        xc = xc + up[:, tap:tap + S] * conv_w[tap]
    xb = xc.reshape(B, S, N_REC_BLOCKS, REC_BLOCK)
    r = jax.nn.sigmoid(jnp.einsum('bsgi,gij->bsgj', xb, w_a).reshape(B, S, D_REC) + b_a)
    i = jax.nn.sigmoid(jnp.einsum('bsgi,gij->bsgj', xb, w_i).reshape(B, S, D_REC) + b_i)
    log_a = -RGLRU_C * r.astype(f32) * jax.nn.softplus(-lam.astype(f32))
    a = jnp.exp(log_a)
    b = jnp.sqrt(-jnp.expm1(2.0 * log_a)) * (i * xc).astype(f32)

    def combine(left, right):
        a_l, b_l = left
        a_r, b_r = right
        return a_l * a_r, a_r * b_l + b_r

    _, h = lax.associative_scan(combine, (a, b), axis=1)
    return (h * jax.nn.gelu(gate.astype(f32))).astype(u.dtype)

def _forgetting_attention(q, k, v, f_logit, b_f, q_norm_w, k_norm_w):
    B, S, _ = q.shape
    f32 = jnp.float32
    q = _rmsnorm(q.reshape(B, S, N_HEADS, HEAD_DIM), q_norm_w).astype(f32)
    k = _rmsnorm(k.reshape(B, S, N_HEADS, HEAD_DIM), k_norm_w).astype(f32)
    v = v.reshape(B, S, N_HEADS, HEAD_DIM).astype(f32)
    log_f = jax.nn.log_sigmoid(f_logit.astype(f32) + b_f.astype(f32))
    c = jnp.cumsum(log_f, axis=1)
    c_k = jnp.transpose(c, (0, 2, 1))
    n_blocks = S // Q_BLOCK
    q_blocks = q.reshape(B, n_blocks, Q_BLOCK, N_HEADS, HEAD_DIM).transpose(1, 0, 2, 3, 4)
    c_blocks = c_k.reshape(B, N_HEADS, n_blocks, Q_BLOCK).transpose(2, 0, 1, 3)
    k_pos = jnp.arange(S)
    scale = HEAD_DIM ** -0.5

    def one_block(args):
        q_blk, c_q, blk = args
        logits = jnp.einsum('bqhd,bkhd->bhqk', q_blk, k) * scale + (c_q[..., :, None] - c_k[:, :, None, :])
        q_pos = blk * Q_BLOCK + jnp.arange(Q_BLOCK)
        causal = q_pos[:, None] >= k_pos[None, :]
        p = jax.nn.softmax(jnp.where(causal, logits, -jnp.inf), axis=-1)
        return jnp.einsum('bhqk,bkhd->bqhd', p, v)

    o = lax.map(one_block, (q_blocks, c_blocks, jnp.arange(n_blocks)))
    return o.transpose(1, 0, 2, 3, 4).reshape(B, S, D_ATT)

def _moe(h, w_router, b_router, w_gate_up, b_gate_up, w_down, b_down):
    B, S, D = h.shape
    f32 = jnp.float32
    T = B * S
    A = T * TOP_K
    xt = h.reshape(T, D)
    logits = (xt @ w_router + b_router).astype(f32)
    top_vals, top_idx = lax.top_k(logits, TOP_K)
    gates = jax.nn.softmax(top_vals, axis=-1)
    flat_e = top_idx.reshape(A)
    order = jnp.argsort(flat_e)
    sorted_e = flat_e[order]
    token = order // TOP_K
    gate_sorted = gates.reshape(A)[order]
    counts = jnp.bincount(flat_e, length=N_EXPERTS)
    group_start = jnp.cumsum(counts) - counts
    padded = (counts + EXPERT_BLOCK - 1) // EXPERT_BLOCK * EXPERT_BLOCK
    pad_end = jnp.cumsum(padded)
    pad_start = pad_end - padded
    dest = pad_start[sorted_e] + jnp.arange(A) - group_start[sorted_e]
    n_blocks = -(-A // EXPERT_BLOCK) + N_EXPERTS
    xs = jnp.zeros((n_blocks * EXPERT_BLOCK, D), xt.dtype).at[dest].set(xt[token])
    block_expert = jnp.minimum(
        jnp.searchsorted(pad_end, jnp.arange(n_blocks) * EXPERT_BLOCK, side='right'), N_EXPERTS - 1)

    def expert_block(args):
        x_blk, e = args
        gu = x_blk @ w_gate_up[e] + b_gate_up[e]
        g = jnp.minimum(gu[:, :D_EXPERT], SWIGLU_LIMIT)
        u = jnp.clip(gu[:, D_EXPERT:], -SWIGLU_LIMIT, SWIGLU_LIMIT)
        act = (u + 1.0) * (g * jax.nn.sigmoid(SWIGLU_ALPHA * g))
        return act @ w_down[e] + b_down[e]

    ys = lax.map(expert_block, (xs.reshape(n_blocks, EXPERT_BLOCK, D), block_expert))
    y = ys.reshape(-1, D)[dest].astype(f32) * gate_sorted[:, None]
    out = jax.ops.segment_sum(y, token, num_segments=T)
    return out.reshape(B, S, D).astype(h.dtype)

def setup_inputs(seed: int = 0) -> dict:
    key = jax.random.key(seed)
    ks = jax.random.split(key, 24)
    f32 = jnp.float32
    L = DEPTH

    def nrm(k, shape, scale):
        return jax.random.normal(k, shape, f32) * scale

    a0 = jax.random.uniform(ks[9], (L, D_REC), f32, 0.9, 0.999)
    sig = a0 ** (1.0 / RGLRU_C)
    rg_lambda = jnp.log(sig) - jnp.log1p(-sig)
    return {
        "x": nrm(ks[0], (BATCH, SEQ, D_MODEL), 1.0),
        "ln1_w": 1.0 + nrm(ks[1], (L, D_MODEL), 0.02),
        "w_in": nrm(ks[2], (L, D_MODEL, D_IN_PROJ), D_MODEL ** -0.5),
        "conv_w": nrm(ks[3], (L, CONV_WIDTH, D_REC), CONV_WIDTH ** -0.5),
        "conv_b": nrm(ks[4], (L, D_REC), 0.02),
        "w_rg_a": nrm(ks[5], (L, N_REC_BLOCKS, REC_BLOCK, REC_BLOCK), REC_BLOCK ** -0.5),
        "b_rg_a": nrm(ks[6], (L, D_REC), 0.02),
        "w_rg_i": nrm(ks[7], (L, N_REC_BLOCKS, REC_BLOCK, REC_BLOCK), REC_BLOCK ** -0.5),
        "b_rg_i": nrm(ks[8], (L, D_REC), 0.02),
        "rg_lambda": rg_lambda,
        "b_forget": jax.random.uniform(ks[10], (L, N_HEADS), f32, 1.0, 4.0),
        "q_norm_w": 1.0 + nrm(ks[11], (L, HEAD_DIM), 0.02),
        "k_norm_w": 1.0 + nrm(ks[12], (L, HEAD_DIM), 0.02),
        "rec_out_norm_w": 1.0 + nrm(ks[13], (L, D_REC), 0.02),
        "attn_out_norm_w": 1.0 + nrm(ks[14], (L, D_ATT), 0.02),
        "w_out": nrm(ks[15], (L, D_MIX, D_MODEL), D_MIX ** -0.5),
        "ln2_w": 1.0 + nrm(ks[16], (L, D_MODEL), 0.02),
        "w_router": nrm(ks[17], (L, D_MODEL, N_EXPERTS), D_MODEL ** -0.5),
        "b_router": nrm(ks[18], (L, N_EXPERTS), 0.01),
        "w_gate_up": nrm(ks[19], (L, N_EXPERTS, D_MODEL, 2 * D_EXPERT), D_MODEL ** -0.5),
        "b_gate_up": nrm(ks[20], (L, N_EXPERTS, 2 * D_EXPERT), 0.02),
        "w_down": nrm(ks[21], (L, N_EXPERTS, D_EXPERT, D_MODEL), D_EXPERT ** -0.5),
        "b_down": nrm(ks[22], (L, N_EXPERTS, D_MODEL), 0.02),
    }

def reference(x, ln1_w, w_in, conv_w, conv_b, w_rg_a, b_rg_a, w_rg_i, b_rg_i, rg_lambda, b_forget,
              q_norm_w, k_norm_w, rec_out_norm_w, attn_out_norm_w, w_out, ln2_w, w_router, b_router,
              w_gate_up, b_gate_up, w_down, b_down):
    o_q = 2 * D_REC
    o_k = o_q + D_ATT
    o_v = o_k + D_ATT
    o_f = o_v + D_ATT
    for l in range(DEPTH):
        h = _rmsnorm(x, ln1_w[l])
        proj = jnp.einsum('bsd,de->bse', h, w_in[l])
        u = proj[..., :D_REC]
        gate = proj[..., D_REC:o_q]
        q = proj[..., o_q:o_k]
        k = proj[..., o_k:o_v]
        v = proj[..., o_v:o_f]
        f_logit = proj[..., o_f:]
        rec = _rg_lru_group(u, gate, conv_w[l], conv_b[l], w_rg_a[l], b_rg_a[l],
                            w_rg_i[l], b_rg_i[l], rg_lambda[l])
        att = _forgetting_attention(q, k, v, f_logit, b_forget[l], q_norm_w[l], k_norm_w[l])
        mix = jnp.concatenate([_rmsnorm(rec, rec_out_norm_w[l]).astype(x.dtype),
                               _rmsnorm(att, attn_out_norm_w[l]).astype(x.dtype)], axis=-1)
        x = x + jnp.einsum('bse,ed->bsd', mix, w_out[l])
        x = x + _moe(_rmsnorm(x, ln2_w[l]), w_router[l], b_router[l], w_gate_up[l], b_gate_up[l],
                     w_down[l], b_down[l])
    return x


_drawn_inputs = setup_inputs


def setup_inputs(seed=0):
    import zlib

    import numpy as np

    out = dict(_drawn_inputs(seed))
    spreads = {}
    factors = {'b_rg_a': 4.714,
     'b_rg_i': 4.983,
     'q_norm_w': 2.759,
     'k_norm_w': 2.759,
     'b_gate_up': 6.825,
     'b_down': 7.832}
    for name, (base, spread) in spreads.items():
        noise = np.random.default_rng([zlib.crc32(name.encode()), seed]).standard_normal(out[name].shape)
        drawn = base * np.exp(spread * noise) if base else spread * noise
        out[name] = __import__('jax').numpy.asarray(drawn.astype(out[name].dtype))
    for name, factor in factors.items():
        out[name] = (out[name] * factor).astype(out[name].dtype)
    return out
```

```python
from contextlib import ExitStack

import concourse.bass as bass
from concourse import mybir

P = 128
D = 1024
S = 1024
T = S // P
KT = D // P
DR = 512
CT = DR // P
H, HD = 8, 64
TAPS = 4
E_, TOPK = 32, 4
CHUNK = 256
NB = CHUNK // P
ITEMS = E_ + TOPK * S // CHUNK
EPS = 1e-6
LIMIT, ALPHA = 7.0, 1.702
F32, F32R, BF16, I32, U32 = (mybir.dt.float32, mybir.dt.float32r, mybir.dt.bfloat16, mybir.dt.int32,
                             mybir.dt.uint32)
ACT = mybir.ActivationFunctionType
ALU = mybir.AluOpType
AX = mybir.AxisListType
KIB = 1024


def f32(ap):
    return ap.bitcast(F32)


class Chain:

    def __init__(self, eng, sem):
        self.eng, self.sem, self.n = eng, sem, 0

    def __call__(self, ins):
        self.n += 1
        ins.then_inc(self.sem, 1)
        self.eng.wait_ge(self.sem, self.n)


def stage_a(nc, m, a):
    with ExitStack() as ctx:
        def at(name, shape, dt, off):
            return nc.alloc_sbuf_tensor_at("A_" + name, shape, dt, offset=m.base + off)

        def sem(name):
            return ctx.enter_context(nc.semaphore("A_" + name))

        def psum(name, shape):
            return ctx.enter_context(nc.psum_tensor("A_" + name, shape, F32))

        h_hi = at("h_hi", [P, KT, S], F32R, 0)
        h_lo = at("h_lo", [P, KT, S], F32R, 32 * KIB)
        x_rows = at("x_rows", [P, T, D], F32, 64 * KIB)
        o = 128 * KIB
        w_st = [at(f"w_st{i}", [P, KT, P], F32, o + 4 * KIB * i) for i in range(3)]
        w_hi = [at(f"w_hi{i}", [P, KT, P], F32R, o + 4 * KIB * (3 + i)) for i in range(2)]
        w_lo = [at(f"w_lo{i}", [P, KT, P], F32R, o + 4 * KIB * (5 + i)) for i in range(2)]
        o += 28 * KIB
        v_hi = at("v_hi", [P, KT, DR], F32R, o)
        v_lo = at("v_lo", [P, KT, DR], F32R, o + 16 * KIB)
        u_pad = at("u_pad", [P, S + TAPS], F32, o)
        conv = at("conv", [P, S], F32, o + 5 * KIB)
        gate = at("gate", [P, S], F32, o + 9 * KIB)
        decay = at("decay", [P, S], F32, o + 13 * KIB)
        denom = at("denom", [P, S], F32, o + 17 * KIB)
        rgate = at("rgate", [P, S], F32, o + 21 * KIB)
        igate = at("igate", [P, S], F32, o + 25 * KIB)
        o += 32 * KIB
        square = at("square", [P, S], F32, o)
        rscale = at("rscale", [P, S], F32, o + 4 * KIB)
        o += 8 * KIB
        wf_st = at("wf_st", [P, KT, H], F32, o)
        wf_hi = at("wf_hi", [P, KT, H], F32R, o + 256)
        wf_lo = at("wf_lo", [P, KT, H], F32R, o + 512)
        wa = at("wa", [P, CT, P], F32, o + 1024)
        wi = at("wi", [P, CT, P], F32, o + 3072)
        o += 5 * KIB
        prm_rows = at("prm_rows", [P, P], F32, 188 * KIB)
        bf = at("bf", [P, H], F32, o)
        prm = m.prm
        sm = at("sm", [P, 512], F32, o + 512)
        ln1 = prm[:, 0:8]
        conv_w = prm[:, 8:24].rearrange("p (a c) -> p a c", a=TAPS)
        conv_b = prm[:, 24:28]
        b_a = prm[:, 28:32]
        b_i = prm[:, 32:36]
        lam = prm[:, 36:40]
        qn = prm[:, 40:41]
        kn = prm[:, 41:42]
        ss = sm[:, 0:8]
        rstd = sm[:, 8:16]
        z = sm[:, 16:80]
        zabs, zexp, zone, zdiff, zmask, zlog = (sm[:, 80 + 64 * i:144 + 64 * i] for i in range(6))
        decay_pos = sm[:, 464:468]
        decay_neg = sm[:, 468:472]

        p_in = [psum(f"p_in{i}", [P, 2, 512]) for i in range(2)]
        p_g = [psum(f"p_g{i}", [P, 2, 512]) for i in range(2)]

        x_in = [sem(f"x_in{t}") for t in range(T)]
        prm_in, prm_mm, prm_s, wblk_in = sem("prm_in"), sem("prm_mm"), sem("prm_s"), sem("wblk_in")
        w_in_s = [sem(f"w_in{i}") for i in range(3)]
        consts = sem("consts")
        zeroed = sem("zeroed")
        squared, rstd_pre, rstd_ok, normed = sem("squared"), sem("rstd_pre"), sem("rstd_ok"), sem("normed")
        turned, h_hi_s, h_lo_s = sem("turned"), sem("h_hi_s"), sem("h_lo_s")
        whi_s, wlo_s = sem("whi_s"), sem("wlo_s")
        fhi_s, flo_s = sem("fhi_s"), sem("flo_s")
        proj_s = sem("proj_s")
        u_s, conv_s, gelu_s = sem("u_s"), sem("conv_s"), sem("gelu_s")
        rg_mm, sig_s, tanh_s, var_s, sqrt_s, rec_s = (sem(n) for n in
                                                      ("rg_mm", "sig_s", "tanh_s", "var_s", "sqrt_s", "rec_s"))
        qk_s, ms_mm, ms_s, rs_s, qkn_s = (sem(n) for n in ("qk_s", "ms_mm", "ms_s", "rs_s", "qkn_s"))
        v_mm, v_act, f_mm = sem("v_mm"), sem("v_act"), sem("f_mm")
        lam_abs, lam_exp, lam_one, lam_log, lam_s = (sem(n) for n in
                                                     ("lam_abs", "lam_exp", "lam_one", "lam_log", "lam_s"))
        dve_step, act_step, pool_step = sem("dve_step"), sem("act_step"), sem("pool_step")

        NW = 20

        def col(n):
            if n < 8:
                return (n // 2) * P + (n % 2) * DR
            return 2 * DR + (n - 8) * P

        block = ctx.enter_context(nc.Block())

        @block.sync
        def _(sp):
            for t in range(T):
                sp.dma_start(x_rows[:, t, :], a.x[0, t * P:(t + 1) * P, :]).then_inc(x_in[t], 16)
                if t % 2 == 1 and t < 6:
                    n = t // 2
                    sp.dma_start(w_st[n][:], a.w_in[0, :, col(n):col(n) + P].rearrange("(k p) n -> p k n", p=P)
                                 ).then_inc(w_in_s[n], 16)
            for n in range(3, NW):
                sp.wait_ge(wlo_s, n - 2)
                sp.dma_start(w_st[n % 3][:], a.w_in[0, :, col(n):col(n) + P].rearrange("(k p) n -> p k n", p=P)
                             ).then_inc(w_in_s[n % 3], 16)

        @block.gpsimd
        def _(pool):
            for row, src in ((0, a.ln1_w[0]), (8, a.conv_w[0].rearrange("t c -> (t c)")), (24, a.conv_b[0]),
                             (28, a.b_rg_a[0]), (32, a.b_rg_i[0]), (36, a.rg_lambda[0]),
                             (42, a.rec_out_norm_w[0]), (46, a.attn_out_norm_w[0])):
                n = src.shape[0] // P
                pool.dma_start(prm_rows[row:row + n, :], src.rearrange("(k p) -> k p", p=P)).then_inc(prm_in, 16)
            for row, src in ((40, a.q_norm_w), (41, a.k_norm_w)):
                for half in range(2):
                    pool.dma_start(prm_rows[row:row + 1, half * HD:(half + 1) * HD], src).then_inc(prm_in, 16)
            pool.dma_start(bf[:], a.b_forget[0:1, :].to_broadcast([P, H])).then_inc(prm_in, 16)
            pool.dma_start(wf_st[:], a.w_in[0, :, 5 * DR:5 * DR + H].rearrange("(k p) n -> p k n", p=P)
                           ).then_inc(prm_in, 16)
            step = Chain(pool, pool_step)
            step(pool.memset(m.ident[:], 0.0))
            step(pool.affine_select(out=m.ident[:], in_=m.ident[:], compare_op=ALU.not_equal, fill=1.0, base=0,
                                    pattern=[[-1, P]], channel_multiplier=1))
            step(pool.tensor_copy(m.ident_b[:], m.ident[:]))
            step(pool.memset(m.head_ones[:], 0.0))
            step(pool.memset(m.head_ones[0:HD, 0:HD], 1.0 / HD))
            step(pool.memset(m.head_ones[HD:P, HD:P], 1.0 / HD))
            step(pool.memset(m.rec_ones[:], 1.0 / DR))
            step(pool.memset(m.mask_b[:], 0.0))
            step(pool.affine_select(out=m.mask_b[:], in_=m.mask_b[:], compare_op=ALU.is_ge, fill=-1e30, base=0,
                                    pattern=[[-1, P]], channel_multiplier=1))
            step(pool.memset(u_pad[:, 0:TAPS], 0.0))
            step(pool.memset(wa[:], 0.0))
            step(pool.memset(wi[:], 0.0))
            pool.memset(sm[:, 480:481], 0.0).then_inc(consts, 1)
            for c in range(CT):
                for half in range(2):
                    lo, hi = half * HD, (half + 1) * HD
                    pool.dma_start(wa[lo:hi, c, lo:hi], a.w_rg_a[0, 2 * c + half]).then_inc(wblk_in, 16)
                    pool.dma_start(wi[lo:hi, c, lo:hi], a.w_rg_i[0, 2 * c + half]).then_inc(wblk_in, 16)

        N_PRM = 14 * 16

        @block.scalar
        def _(act):
            step = Chain(act, act_step)

            def split_hi(n):
                act.wait_ge(w_in_s[n % 3], 16 * (n // 3 + 1))
                if n < 16:
                    if n >= 2:
                        act.wait_ge(proj_s, n - 1)
                    act.activation(w_hi[n % 2][:], w_st[n % 3][:], ACT.Copy).then_inc(whi_s, 1)
                else:
                    if n == 16:
                        act.wait_ge(rec_s, CT)
                    act.activation(v_hi[:, :, (n - 16) * P:(n - 15) * P], w_st[n % 3][:], ACT.Copy).then_inc(whi_s, 1)

            for t in range(T):
                act.wait_ge(x_in[t], 16)
                if t >= 2:
                    act.wait_ge(squared, t - 1)
                act.activation(p_g[t % 2][:].rearrange("p a b -> p (a b)"), x_rows[:, t, :], ACT.Square,
                               accum_out=ss[:, t:t + 1]).then_inc(squared, 1)
            act.wait_ge(rstd_pre, 1)
            act.activation(rstd, ss, ACT.Sqrt).then_inc(rstd_ok, 1)
            split_hi(0)
            split_hi(1)
            act.wait_ge(prm_s, 1)
            for g in range(2 * KT):
                k, half = g // 2, g % 2
                act.wait_ge(turned, g + 1)
                act.activation(h_hi[:, k, half * 512:(half + 1) * 512], p_in[g % 2][:, 0, :], ACT.Copy,
                               scale=ln1[:, k:k + 1]).then_inc(h_hi_s, 1)
            act.wait_ge(lam_abs, 1)
            act.activation(zexp[:, 0:CT], zabs[:, 0:CT], ACT.Exp, scale=-1.0).then_inc(lam_exp, 1)
            act.wait_ge(lam_one, 1)
            act.activation(zlog[:, 0:CT], zone[:, 0:CT], ACT.Ln).then_inc(lam_log, 1)
            act.activation(wf_hi[:], wf_st[:], ACT.Copy).then_inc(fhi_s, 1)
            for n in range(16):
                act.wait_ge(proj_s, n + 1)
                split_hi(n + 2)
                pin = p_in[n % 2][:].rearrange("p a b -> p (a b)")
                c = n // 2
                if n < 8 and n % 2 == 0:
                    act.wait_ge(consts, 1)
                    if c:
                        act.wait_ge(conv_s, c)
                    act.activation(u_pad[:, TAPS - 1:TAPS - 1 + S], pin, ACT.Copy).then_inc(u_s, 1)
                elif n < 8:
                    if c:
                        act.wait_ge(rec_s, c)
                    act.activation(gate[:], pin, ACT.Gelu_apprx_tanh).then_inc(gelu_s, 1)
                    act.wait_ge(rg_mm, c + 1)
                    act.activation(rgate[:], p_g[0][:].rearrange("p a b -> p (a b)"), ACT.Sigmoid,
                                   bias=b_a[:, c:c + 1]).then_inc(sig_s, 1)
                    act.activation(igate[:], p_g[1][:].rearrange("p a b -> p (a b)"), ACT.Sigmoid,
                                   bias=b_i[:, c:c + 1]).then_inc(sig_s, 1)
                    act.wait_ge(lam_s, 1)
                    act.wait_ge(sig_s, 2 * c + 1)
                    step(act.activation(decay[:], rgate[:], ACT.Exp, scale=decay_neg[:, c:c + 1]))
                    act.activation(rgate[:], rgate[:], ACT.Tanh, scale=decay_pos[:, c:c + 1]).then_inc(tanh_s, 1)
                    act.wait_ge(var_s, c + 1)
                    act.activation(denom[:], denom[:], ACT.Sqrt).then_inc(sqrt_s, 1)
                else:
                    j = n - 8
                    if j:
                        act.wait_ge(ms_mm, j)
                    act.activation(square[:], pin, ACT.Square).then_inc(act_step, 1)
                    step.n += 1
                    act.activation(m.qk[:, j, :], pin, ACT.Copy).then_inc(qk_s, 1)
                    if j:
                        act.wait_ge(ms_s, j)
                        act.activation(rscale[:], rscale[:], ACT.Sqrt).then_inc(rs_s, 1)
            for n in (18, 19):
                split_hi(n)
            act.wait_ge(ms_s, 8)
            act.activation(rscale[:], rscale[:], ACT.Sqrt).then_inc(rs_s, 1)
            for t in range(T):
                act.wait_ge(v_mm, t + 1)
                act.activation(m.v[:, t, :], p_in[(t // 2) % 2][:, t % 2, :], ACT.Copy).then_inc(v_act, 1)
            act.wait_ge(lam_abs, 2)
            act.activation(zexp, zabs, ACT.Exp, scale=-1.0).then_inc(lam_exp, 1)
            act.wait_ge(lam_one, 2)
            act.activation(zlog, zone, ACT.Ln).then_inc(lam_log, 1)

        @block.vector
        def _(dve):
            step = Chain(dve, dve_step)

            def split_lo(n):
                dve.wait_ge(whi_s, n + 1)
                hi = w_hi[n % 2][:] if n < 16 else v_hi[:, :, (n - 16) * P:(n - 15) * P]
                lo = w_lo[n % 2][:] if n < 16 else v_lo[:, :, (n - 16) * P:(n - 15) * P]
                dve.tensor_tensor(lo, w_st[n % 3][:], f32(hi), ALU.subtract).then_inc(wlo_s, 1)

            def log1p_exp(w, turn):
                e, one, diff, mask, log = (q[:, 0:w] for q in (zexp, zone, zdiff, zmask, zlog))
                dve.wait_ge(lam_exp, turn)
                dve.tensor_scalar(one, e, 1.0, None, ALU.add).then_inc(lam_one, 1)
                dve.wait_ge(lam_one, turn)
                step(dve.tensor_scalar(diff, one, -1.0, None, ALU.add))
                step(dve.tensor_scalar(mask, diff, 0.0, None, ALU.is_equal))
                step(dve.tensor_tensor(diff, diff, mask, ALU.add))
                step(dve.reciprocal(diff, diff))
                step(dve.tensor_tensor(diff, diff, e, ALU.mult))
                step(dve.tensor_tensor(mask, mask, e, ALU.mult))
                dve.wait_ge(lam_log, turn)
                step(dve.tensor_tensor(log, log, diff, ALU.mult))
                step(dve.tensor_tensor(log, log, mask, ALU.add))

            dve.wait_ge(squared, T)
            step(dve.tensor_scalar(ss, ss, 1.0 / D, EPS, ALU.mult, ALU.add))
            dve.reciprocal(ss, ss).then_inc(rstd_pre, 1)
            dve.wait_ge(rstd_ok, 1)
            for t in range(T):
                dve.tensor_scalar(x_rows[:, t, :], x_rows[:, t, :], rstd[:, t:t + 1], None,
                                  ALU.mult).then_inc(normed, 1)
            split_lo(0)
            split_lo(1)
            dve.wait_ge(prm_mm, 1)
            dve.tensor_copy(prm[:], p_g[1][:, 1, 0:50]).then_inc(prm_s, 1)
            dve.wait_ge(prm_s, 1)
            step(dve.tensor_scalar(qn, qn, float(HD) ** -0.5, None, ALU.mult))
            for g in range(2 * KT):
                k, half = g // 2, g % 2
                dve.wait_ge(h_hi_s, g + 1)
                dve.scalar_tensor_tensor(out=h_lo[:, k, half * 512:(half + 1) * 512], in0=p_in[g % 2][:, 0, :],
                                         scalar=ln1[:, k:k + 1], in1=f32(h_hi[:, k, half * 512:(half + 1) * 512]),
                                         op0=ALU.mult, op1=ALU.subtract).then_inc(h_lo_s, 1)
            step(dve.tensor_scalar(zdiff[:, 0:CT], lam, -1.0, None, ALU.mult))
            dve.tensor_tensor(zabs[:, 0:CT], zdiff[:, 0:CT], lam, ALU.max).then_inc(lam_abs, 1)
            step(dve.tensor_scalar(z[:, 0:CT], zdiff[:, 0:CT], 0.0, None, ALU.max))
            log1p_exp(CT, 1)
            step(dve.tensor_tensor(z[:, 0:CT], z[:, 0:CT], zlog[:, 0:CT], ALU.add))
            step(dve.tensor_scalar(decay_pos, z[:, 0:CT], 8.0, None, ALU.mult))
            dve.tensor_scalar(decay_neg, z[:, 0:CT], -8.0, None, ALU.mult).then_inc(lam_s, 1)
            dve.wait_ge(fhi_s, 1)
            dve.tensor_tensor(wf_lo[:], wf_st[:], f32(wf_hi[:]), ALU.subtract).then_inc(flo_s, 1)

            def norm_qk(j):
                dve.wait_ge(ms_mm, j + 1)
                step(dve.tensor_scalar(rscale[:], p_g[0][:].rearrange("p a b -> p (a b)"), EPS, None, ALU.add))
                dve.reciprocal(rscale[:], rscale[:]).then_inc(ms_s, 1)
                dve.wait_ge(rs_s, j + 1)
                dve.wait_ge(qk_s, j + 1)
                step(dve.scalar_tensor_tensor(out=m.qk[:, j, :], in0=m.qk[:, j, :], scalar=(qn if j < 4 else kn),
                                              in1=rscale[:], op0=ALU.mult, op1=ALU.mult))

            for n in range(16):
                split_lo(n + 2)
                c = n // 2
                if n < 8 and n % 2 == 0:
                    dve.wait_ge(u_s, c + 1)
                    for tap in range(TAPS):
                        src = u_pad[:, tap:tap + S]
                        w = conv_w[:, tap, c:c + 1]
                        if tap == 0:
                            ins = dve.tensor_scalar(conv[:], src, w, conv_b[:, c:c + 1], ALU.mult, ALU.add)
                        else:
                            ins = dve.scalar_tensor_tensor(out=conv[:], in0=src, scalar=w, in1=conv[:],
                                                           op0=ALU.mult, op1=ALU.add)
                        if tap < TAPS - 1:
                            step(ins)
                        else:
                            ins.then_inc(conv_s, 1)
                elif n < 8:
                    dve.wait_ge(sig_s, 2 * c + 2)
                    dve.wait_ge(conv_s, c + 1)
                    step(dve.tensor_tensor(igate[:], igate[:], conv[:], ALU.mult))
                    dve.wait_ge(tanh_s, c + 1)
                    step(dve.tensor_scalar(denom[:], rgate[:], 1.0, None, ALU.add))
                    step(dve.reciprocal(denom[:], denom[:]))
                    dve.scalar_tensor_tensor(out=denom[:], in0=rgate[:], scalar=2.0, in1=denom[:],
                                             op0=ALU.mult, op1=ALU.mult).then_inc(var_s, 1)
                    dve.wait_ge(sqrt_s, c + 1)
                    step(dve.tensor_tensor(igate[:], igate[:], denom[:], ALU.mult))
                    dve.wait_ge(act_step, c + 1)
                    step(dve.tensor_tensor_scan(out=rgate[:], data0=decay[:], data1=igate[:], initial=0.0,
                                                op0=ALU.mult, op1=ALU.add))
                    dve.wait_ge(gelu_s, c + 1)
                    dve.tensor_tensor(m.rec[:, c, :], rgate[:], gate[:], ALU.mult).then_inc(rec_s, 1)
                elif n > 8:
                    norm_qk(n - 9)
            split_lo(18)
            split_lo(19)
            norm_qk(7)
            dve.wait_ge(f_mm, 1)
            zz = z.rearrange("p (t h) -> p t h", h=H)
            step(dve.tensor_tensor(zz, p_g[1][:, 0, 0:T * H].rearrange("p (t h) -> p t h", h=H),
                                   bf[:].unsqueeze(1).to_broadcast([P, T, H]), ALU.add))
            step(dve.tensor_scalar(zdiff, z, -1.0, None, ALU.mult))
            dve.tensor_tensor(zabs, zdiff, z, ALU.max).then_inc(lam_abs, 1)
            step(dve.tensor_scalar(z, z, 0.0, None, ALU.min))
            log1p_exp(T * H, 2)
            step(dve.tensor_tensor(m.logf[:], z, zlog, ALU.subtract))

        @block.tensor
        def _(pe):
            def three(out, hi, lo, xhi, xlo, first, last):
                pe.matmul(out, hi, xhi, start=first, stop=False)
                pe.matmul(out, hi, xlo, start=False, stop=False)
                return pe.matmul(out, lo, xhi, start=False, stop=last)

            pe.wait_ge(consts, 1)
            pe.wait_ge(prm_in, N_PRM)
            pe.wait_ge(squared, T)
            pe.transpose(p_g[1][:, 1, 0:50], prm_rows[0:50, :], m.ident[0:50, 0:50]).then_inc(prm_mm, 1)
            for g in range(2 * KT):
                k, half = g // 2, g % 2
                pe.wait_ge(normed, 4 * half + 4)
                if g >= 2:
                    pe.wait_ge(h_lo_s, g - 1)
                for t in range(4):
                    ins = pe.transpose(p_in[g % 2][:, 0, t * P:(t + 1) * P],
                                       x_rows[:, 4 * half + t, k * P:(k + 1) * P], m.ident[:])
                ins.then_inc(turned, 1)

            def project(n):
                pe.wait_ge(wlo_s, n + 1)
                if n == 0:
                    pe.wait_ge(h_lo_s, 2 * KT)
                if n >= 2:
                    q = n - 2
                    if q < 8:
                        pe.wait_ge(u_s if q % 2 == 0 else gelu_s, q // 2 + 1)
                    else:
                        pe.wait_ge(qk_s, q - 7)
                for half in range(2):
                    for k in range(KT):
                        r = slice(half * 512, (half + 1) * 512)
                        ins = three(p_in[n % 2][:, half, :], w_hi[n % 2][:, k, :], w_lo[n % 2][:, k, :],
                                    h_hi[:, k, r], h_lo[:, k, r], k == 0, k == KT - 1)
                ins.then_inc(proj_s, 1)

            def mean_squares(j):
                pe.wait_ge(act_step, CT + j + 1)
                if j:
                    pe.wait_ge(ms_s, j)
                for half in range(2):
                    ins = pe.matmul(p_g[0][:, half, :], m.head_ones[:], square[:, half * 512:(half + 1) * 512],
                                    start=True, stop=True)
                ins.then_inc(ms_mm, 1)

            for n in range(16):
                project(n)
                if n < 8 and n % 2 == 1:
                    c = n // 2
                    if c == 0:
                        pe.wait_ge(wblk_in, 16 * 4 * CT)
                    else:
                        pe.wait_ge(sig_s, 2 * c)
                    pe.wait_ge(conv_s, c + 1)
                    for g, w in enumerate((wa, wi)):
                        for half in range(2):
                            ins = pe.matmul(p_g[g][:, half, :], w[:, c, :], conv[:, half * 512:(half + 1) * 512],
                                            start=True, stop=True)
                    ins.then_inc(rg_mm, 1)
                if n > 8:
                    mean_squares(n - 9)
            pe.wait_ge(flo_s, 1)
            for t in range(T):
                for k in range(KT):
                    r = slice(t * P, (t + 1) * P)
                    o_ = p_g[1][:, 0, t * H:(t + 1) * H]
                    pe.matmul(o_, h_hi[:, k, r], wf_hi[:, k, :], start=k == 0, stop=False)
                    pe.matmul(o_, h_hi[:, k, r], wf_lo[:, k, :], start=False, stop=False)
                    ins = pe.matmul(o_, h_lo[:, k, r], wf_hi[:, k, :], start=False, stop=k == KT - 1)
            ins.then_inc(f_mm, 1)
            mean_squares(7)
            pe.wait_ge(wlo_s, NW)
            pe.wait_ge(qk_s, 8)
            for t in range(T):
                if t >= 4:
                    pe.wait_ge(v_act, t - 3)
                for k in range(KT):
                    r = slice(t * P, (t + 1) * P)
                    o_ = p_in[(t // 2) % 2][:, t % 2, :]
                    pe.matmul(o_, h_hi[:, k, r], v_hi[:, k, :], start=k == 0, stop=False)
                    pe.matmul(o_, h_hi[:, k, r], v_lo[:, k, :], start=False, stop=False)
                    ins = pe.matmul(o_, h_lo[:, k, r], v_hi[:, k, :], start=False, stop=k == KT - 1)
                ins.then_inc(v_mm, 1)


def stage_b(nc, m, a):
    with ExitStack() as ctx:
        def at(name, shape, dt, off):
            return nc.alloc_sbuf_tensor_at("B_" + name, shape, dt, offset=m.base + off)

        def sem(name):
            return ctx.enter_context(nc.semaphore("B_" + name))

        c_key = at("c_key", [P, H, S], F32, 0)
        scores = [at(f"scores{i}", [P, S], F32, (48 + 4 * i) * KIB) for i in range(3)]
        wo_st = at("wo_st", [P, D], F32, 60 * KIB)
        probs_t = [at(f"probs_t{i}", [P, S], F32, (128 + 4 * i) * KIB) for i in range(2)]
        ones = at("ones", [P, 512], F32, 200 * KIB)
        top = at("top", [P, T * H], F32, 202 * KIB)
        neg_top = at("neg_top", [P, T * H], F32, 202 * KIB + 256)
        row_inv = at("row_inv", [P, T * H], F32, 202 * KIB + 512)

        p_s = [ctx.enter_context(nc.psum_tensor(f"B_p_s{i}", [P, S], F32)) for i in range(2)]
        p_t = ctx.enter_context(nc.psum_tensor("B_p_t", [P, S], F32))
        p_o = [ctx.enter_context(nc.psum_tensor(f"B_p_o{i}", [P, DR], F32)) for i in range(2)]

        ones_s, cs_mm, cs_s = sem("ones_s"), sem("cs_mm"), sem("cs_s")
        score_mm, score_s, neg_s, exp_s = sem("score_mm"), sem("score_s"), sem("neg_s"), sem("exp_s")
        turn_mm, turn_act, turn_dve, pv_mm = sem("turn_mm"), sem("turn_act"), sem("turn_dve"), sem("pv_mm")
        o_s, wo_in, wo_hi_s, wo_lo_s = sem("o_s"), sem("wo_in"), sem("wo_hi_s"), sem("wo_lo_s")
        dve_step = sem("dve_step")
        steps = [(i, h) for i in range(T) for h in range(H)]
        NS = len(steps)
        WO_AT = {8 * k + 4: k for k in range(KT)}

        block = ctx.enter_context(nc.Block())

        @block.sync
        def _(sp):
            for k in range(KT):
                if k:
                    sp.wait_ge(wo_lo_s, k)
                sp.dma_start(wo_st[:], a.w_out[0, k * P:(k + 1) * P, :]).then_inc(wo_in, 16)

        @block.tensor
        def _(pe):
            for g in range(2 * H):
                h, half = g // 2, g % 2
                if g >= 2:
                    pe.wait_ge(cs_s, g - 1)
                for t in range(4):
                    q = (4 * half + t) * H + h
                    ins = pe.matmul(p_s[g % 2][:, t * P:(t + 1) * P], m.logf[:, q:q + 1].to_broadcast([P, P]),
                                    m.ident[:], start=True, stop=True)
                ins.then_inc(cs_mm, 1)
            pe.wait_ge(cs_s, 2 * H)

            def score(n):
                i, h = steps[n]
                r = slice((h % 2) * HD, (h % 2 + 1) * HD)
                if n >= 2:
                    pe.wait_ge(score_s, n - 1)
                L = P * (i + 1)
                for c0 in range(0, L, 512):
                    c1 = min(c0 + 512, L)
                    ins = pe.matmul(p_s[n % 2][:, c0:c1], m.qk[r, h // 2, i * P:(i + 1) * P],
                                    m.qk[r, CT + h // 2, c0:c1], start=True, stop=True)
                pe.matmul(p_s[n % 2][:, L - P:L], m.ident_b[:], m.mask_b[:], start=False, stop=True,
                          skip_group_check=True).then_inc(score_mm, 1)

            def turn(n):
                i, h = steps[n]
                pe.wait_ge(exp_s, n + 1)
                if n:
                    if (n - 1) % 2:
                        pe.wait_ge(turn_dve, n // 2)
                    else:
                        pe.wait_ge(turn_act, (n + 1) // 2)
                for b in range(i + 1):
                    ins = pe.transpose(p_t[:, b * P:(b + 1) * P], scores[n % 3][:, b * P:(b + 1) * P], m.ident[:])
                ins.then_inc(turn_mm, 1)

            def weigh(n):
                i, h = steps[n]
                if n % 2:
                    pe.wait_ge(turn_dve, (n + 1) // 2)
                else:
                    pe.wait_ge(turn_act, n // 2 + 1)
                if h == 0 and i >= 2:
                    pe.wait_ge(o_s, i - 1)
                for b in range(i + 1):
                    ins = pe.matmul(p_o[i % 2][:, h * HD:(h + 1) * HD], probs_t[n % 2][:, b * P:(b + 1) * P],
                                    m.v[:, b, h * HD:(h + 1) * HD], start=b == 0, stop=b == i)
                ins.then_inc(pv_mm, 1)

            score(0)
            for n in range(NS):
                if n + 1 < NS:
                    score(n + 1)
                turn(n)
                if n:
                    weigh(n - 1)
            weigh(NS - 1)

        @block.scalar
        def _(act):
            for n in range(NS):
                i, h = steps[n]
                L = P * (i + 1)
                act.wait_ge(neg_s, n + 1)
                act.activation(scores[n % 3][:, 0:L], scores[n % 3][:, 0:L], ACT.Exp, bias=neg_top[:, n:n + 1],
                               accum_out=m.row_sum[:, n:n + 1]).then_inc(exp_s, 1)
                if n % 2 == 0:
                    act.wait_ge(turn_mm, n + 1)
                    if n >= 2:
                        act.wait_ge(pv_mm, n - 1)
                    act.activation(probs_t[n % 2][:, 0:L], p_t[:, 0:L], ACT.Copy).then_inc(turn_act, 1)
                if n in WO_AT:
                    k = WO_AT[n]
                    act.wait_ge(wo_in, 16 * (k + 1))
                    act.activation(m.wo_hi[:, k, :], wo_st[:], ACT.Copy).then_inc(wo_hi_s, 1)

        @block.vector
        def _(dve):
            step = Chain(dve, dve_step)
            dve.memset(ones[:], 1.0).then_inc(ones_s, 1)
            dve.wait_ge(ones_s, 1)
            for g in range(2 * H):
                h, half = g // 2, g % 2
                dve.wait_ge(cs_mm, g + 1)
                if half:
                    dve.wait_ge(cs_s, g)
                dve.tensor_tensor_scan(out=c_key[:, h, half * 512:(half + 1) * 512], data0=ones[:],
                                       data1=p_s[g % 2][:, 0:512],
                                       initial=(c_key[:, h, 511:512] if half else 0.0),
                                       op0=ALU.mult, op1=ALU.add).then_inc(cs_s, 1)

            def subtract(n):
                i, h = steps[n]
                L = P * (i + 1)
                dve.wait_ge(score_mm, n + 1)
                if n >= 3:
                    dve.wait_ge(turn_mm, n - 2)
                dve.tensor_tensor_reduce(out=scores[n % 3][:, 0:L], in0=p_s[n % 2][:, 0:L], in1=c_key[:, h, 0:L],
                                         scale=1.0, scalar=-3.0e38, op0=ALU.subtract, op1=ALU.max,
                                         accum_out=top[:, n:n + 1]).then_inc(score_s, 1)
                dve.wait_ge(score_s, n + 1)
                dve.tensor_scalar(neg_top[:, n:n + 1], top[:, n:n + 1], -1.0, None, ALU.mult).then_inc(neg_s, 1)

            def out_rows(i):
                dve.wait_ge(exp_s, H * (i + 1))
                step(dve.reciprocal(row_inv[:, i * H:(i + 1) * H], m.row_sum[:, i * H:(i + 1) * H]))
                dve.wait_ge(pv_mm, H * (i + 1))
                dve.tensor_tensor(m.att[:, i, :].rearrange("p (h d) -> p h d", h=H),
                                  p_o[i % 2][:].rearrange("p (h d) -> p h d", h=H),
                                  row_inv[:, i * H:(i + 1) * H].unsqueeze(2).to_broadcast([P, H, HD]),
                                  ALU.mult).then_inc(o_s, 1)

            subtract(0)
            for n in range(NS):
                if n + 1 < NS:
                    subtract(n + 1)
                i, h = steps[n]
                if n % 2:
                    dve.wait_ge(turn_mm, n + 1)
                    if n >= 2:
                        dve.wait_ge(pv_mm, n - 1)
                    dve.tensor_copy(probs_t[n % 2][:, 0:P * (i + 1)], p_t[:, 0:P * (i + 1)]).then_inc(turn_dve, 1)
                if h == 2 and i:
                    out_rows(i - 1)
                if n in WO_AT:
                    k = WO_AT[n]
                    dve.wait_ge(wo_hi_s, k + 1)
                    dve.tensor_tensor(m.wo_lo[:, k, :], wo_st[:], f32(m.wo_hi[:, k, :]), ALU.subtract).then_inc(wo_lo_s, 1)
            out_rows(T - 1)


def stage_c(nc, m, a):
    with ExitStack() as ctx:
        def at(name, shape, dt, off):
            return nc.alloc_sbuf_tensor_at("C_" + name, shape, dt, offset=m.base + off)

        def sem(name):
            return ctx.enter_context(nc.semaphore("C_" + name))

        mix_hi = at("mix_hi", [P, 2 * CT, S], F32R, 0)
        mix_lo = at("mix_lo", [P, 2 * CT, S], F32R, 64 * KIB)
        x_res = [at(f"x_res{i}", [P, D], F32, (48 + 4 * i) * KIB) for i in range(2)]
        ln2_row = at("ln2_row", [P, D], F32, 56 * KIB)
        w_router = at("w_router", [P, KT, E_], F32, 60 * KIB)
        br_row = at("br_row", [P, E_], F32, 61 * KIB)
        bin_ = at("bin", [P, DR], F32, 62 * KIB)
        h2t = [at(f"h2t{i}", [P, KT, P], F32, (96 + 4 * i) * KIB) for i in range(2)]
        x2 = [at(f"x2{i}", [P, D], F32, (104 + 4 * i) * KIB) for i in range(2)]
        h2 = [at(f"h2{i}", [P, D], F32, (128 + 4 * i) * KIB) for i in range(2)]
        rec_sq = at("rec_sq", [P, S], F32, 104 * KIB)
        rec_rs = at("rec_rs", [P, S], F32, 108 * KIB)
        sm = at("sm", [P, 64], F32, 200 * KIB)
        att_ss, att_rs, x2_ss, x2_rs = (sm[:, 8 * i:8 * i + 8] for i in range(4))
        rec_w, att_w = m.prm[:, 42:46], m.prm[:, 46:50]

        p_m = [ctx.enter_context(nc.psum_tensor(f"C_p_m{i}", [P, 512], F32)) for i in range(2)]
        p_o = [ctx.enter_context(nc.psum_tensor(f"C_p_o{i}", [P, D], F32)) for i in range(2)]
        p_l = ctx.enter_context(nc.psum_tensor("C_p_l", [P, E_], F32))

        in_s, x_in = sem("in_s"), [sem(f"x_in{i}") for i in range(2)]
        att_sq, att_pre, att_ok, att_n = sem("att_sq"), sem("att_pre"), sem("att_ok"), sem("att_n")
        sq_s, ms_mm, rs_pre, rs_ok = sem("sq_s"), sem("ms_mm"), sem("rs_pre"), sem("rs_ok")
        rec_n, mix_hi_s, mix_lo_s, turned = sem("rec_n"), sem("mix_hi_s"), sem("mix_lo_s"), sem("turned")
        out_mm, x2_s, x2_sq, x2_pre, x2_ok = (sem(n) for n in ("out_mm", "x2_s", "x2_sq", "x2_pre", "x2_ok"))
        h2_s, h2_mm, h2t_s, log_mm, log_s = (sem(n) for n in ("h2_s", "h2_mm", "h2t_s", "log_mm", "log_s"))
        x2_out, h2_out = [sem(f"x2_out{i}") for i in range(2)], [sem(f"h2_out{i}") for i in range(2)]
        dve_step = sem("dve_step")

        block = ctx.enter_context(nc.Block())

        @block.sync
        def _(sp):
            sp.dma_start(ln2_row[:], a.ln2_w[0:1, :].to_broadcast([P, D])).then_inc(in_s, 16)
            sp.dma_start(w_router[:], a.w_router[0].rearrange("(k p) n -> p k n", p=P)).then_inc(in_s, 16)
            sp.dma_start(br_row[:], a.b_router[0:1, :].to_broadcast([P, E_])).then_inc(in_s, 16)
            for t in range(T + 2):
                if t < T:
                    if t >= 2:
                        sp.wait_ge(x2_s, t - 1)
                    sp.dma_start(x_res[t % 2][:], a.x[0, t * P:(t + 1) * P, :]).then_inc(x_in[t % 2], 16)
                if t >= 2:
                    q = t - 2
                    sp.wait_ge(x2_s, q + 1)
                    sp.dma_start(m.x2_d[q * P:(q + 1) * P, :], x2[q % 2][:]).then_inc(x2_out[q % 2], 16)
                    sp.wait_ge(h2_s, q + 1)
                    sp.dma_start(m.h2_d[q * P:(q + 1) * P, :], h2[q % 2][:]).then_inc(h2_out[q % 2], 16)
            for i in range(2):
                sp.wait_ge(x2_out[i], 16 * (T // 2))
                sp.wait_ge(h2_out[i], 16 * (T // 2))

        @block.scalar
        def _(act):
            for t in range(T):
                if t:
                    act.wait_ge(att_sq, t)
                act.activation(bin_[:], m.att[:, t, :], ACT.Square, accum_out=att_ss[:, t:t + 1]).then_inc(att_sq, 1)
            for c in range(CT):
                if c:
                    act.wait_ge(ms_mm, c)
                act.activation(rec_sq[:], m.rec[:, c, :], ACT.Square).then_inc(sq_s, 1)
            act.wait_ge(att_pre, 1)
            act.activation(att_rs, att_ss, ACT.Sqrt).then_inc(att_ok, 1)
            act.wait_ge(rs_pre, 2)
            act.activation(rec_rs[:], rec_rs[:], ACT.Sqrt).then_inc(rs_ok, 1)
            for g in range(CT):
                act.wait_ge(rec_n, g + 1)
                act.activation(mix_hi[:, g, :], m.rec[:, g, :], ACT.Copy).then_inc(mix_hi_s, 1)
            for g in range(2 * CT):
                c, half = g % CT, g // CT
                act.wait_ge(turned, g + 1)
                act.activation(mix_hi[:, CT + c, half * 512:(half + 1) * 512], p_m[g % 2][:], ACT.Copy,
                               scale=att_w[:, c:c + 1]).then_inc(mix_hi_s, 1)
            for t in range(T):
                act.wait_ge(x2_s, t + 1)
                if t:
                    act.wait_ge(x2_sq, t)
                    act.wait_ge(h2_s, t)
                if t >= 2:
                    act.wait_ge(h2_mm, t - 1)
                    act.wait_ge(h2_out[t % 2], 16 * (t // 2))
                act.activation(h2[t % 2][:], x2[t % 2][:], ACT.Square, accum_out=x2_ss[:, t:t + 1]).then_inc(x2_sq, 1)
                act.wait_ge(x2_pre, t + 1)
                act.activation(x2_rs[:, t:t + 1], x2_ss[:, t:t + 1], ACT.Sqrt).then_inc(x2_ok, 1)
                act.wait_ge(h2_mm, t + 1)
                if t >= 2:
                    act.wait_ge(log_mm, t - 1)
                act.activation(h2t[t % 2][:, 0:4, :].rearrange("p k n -> p (k n)"), p_m[0][:], ACT.Copy).then_inc(h2t_s, 1)
                act.activation(h2t[t % 2][:, 4:8, :].rearrange("p k n -> p (k n)"), p_m[1][:], ACT.Copy).then_inc(h2t_s, 1)

        @block.vector
        def _(dve):
            step = Chain(dve, dve_step)
            dve.wait_ge(att_sq, T)
            step(dve.tensor_scalar(att_ss, att_ss, 1.0 / DR, EPS, ALU.mult, ALU.add))
            dve.reciprocal(att_ss, att_ss).then_inc(att_pre, 1)
            dve.wait_ge(att_ok, 1)
            for t in range(T):
                dve.tensor_scalar(m.att[:, t, :], m.att[:, t, :], att_rs[:, t:t + 1], None, ALU.mult).then_inc(att_n, 1)
            dve.wait_ge(ms_mm, CT)
            for half in range(2):
                r = slice(half * 512, (half + 1) * 512)
                step(dve.tensor_scalar(rec_rs[:, r], p_o[0][:, r], EPS, None, ALU.add))
                dve.reciprocal(rec_rs[:, r], rec_rs[:, r]).then_inc(rs_pre, 1)
            dve.wait_ge(rs_ok, 1)
            for c in range(CT):
                dve.scalar_tensor_tensor(out=m.rec[:, c, :], in0=m.rec[:, c, :], scalar=rec_w[:, c:c + 1],
                                         in1=rec_rs[:], op0=ALU.mult, op1=ALU.mult).then_inc(rec_n, 1)
            for c in range(CT):
                dve.wait_ge(mix_hi_s, c + 1)
                dve.tensor_tensor(mix_lo[:, c, :], m.rec[:, c, :], f32(mix_hi[:, c, :]), ALU.subtract).then_inc(mix_lo_s, 1)
            for g in range(2 * CT):
                c, half = g % CT, g // CT
                r = slice(half * 512, (half + 1) * 512)
                dve.wait_ge(mix_hi_s, CT + g + 1)
                dve.scalar_tensor_tensor(out=mix_lo[:, CT + c, r], in0=p_m[g % 2][:], scalar=att_w[:, c:c + 1],
                                         in1=f32(mix_hi[:, CT + c, r]), op0=ALU.mult, op1=ALU.subtract).then_inc(mix_lo_s, 1)
            dve.wait_ge(in_s, 48)

            def logits(t):
                dve.wait_ge(log_mm, t + 1)
                dve.tensor_tensor(m.logits[:, t, :], p_l[:], br_row[:], ALU.add).then_inc(log_s, 1)

            for t in range(T):
                dve.wait_ge(out_mm, t + 1)
                dve.wait_ge(x_in[t % 2], 16 * (t // 2 + 1))
                if t >= 2:
                    dve.wait_ge(x2_out[t % 2], 16 * (t // 2))
                dve.tensor_tensor(x2[t % 2][:], p_o[t % 2][:], x_res[t % 2][:], ALU.add).then_inc(x2_s, 1)
                dve.wait_ge(x2_sq, t + 1)
                step(dve.tensor_scalar(x2_ss[:, t:t + 1], x2_ss[:, t:t + 1], 1.0 / D, EPS, ALU.mult, ALU.add))
                dve.reciprocal(x2_ss[:, t:t + 1], x2_ss[:, t:t + 1]).then_inc(x2_pre, 1)
                dve.wait_ge(x2_ok, t + 1)
                dve.scalar_tensor_tensor(out=h2[t % 2][:], in0=x2[t % 2][:], scalar=x2_rs[:, t:t + 1], in1=ln2_row[:],
                                         op0=ALU.mult, op1=ALU.mult).then_inc(h2_s, 1)
                if t:
                    logits(t - 1)
            logits(T - 1)

        @block.tensor
        def _(pe):
            for c in range(CT):
                pe.wait_ge(sq_s, c + 1)
                for half in range(2):
                    r = slice(half * 512, (half + 1) * 512)
                    ins = pe.matmul(p_o[0][:, r], m.rec_ones[:], rec_sq[:, r], start=c == 0, stop=c == CT - 1)
                ins.then_inc(ms_mm, 1)
            for g in range(2 * CT):
                c, half = g % CT, g // CT
                pe.wait_ge(att_n, 4 * half + 4)
                if g >= 2:
                    pe.wait_ge(mix_lo_s, CT + g - 1)
                for t in range(4):
                    ins = pe.transpose(p_m[g % 2][:, t * P:(t + 1) * P], m.att[:, 4 * half + t, c * P:(c + 1) * P],
                                       m.ident[:])
                ins.then_inc(turned, 1)

            def project(t):
                pe.wait_ge(mix_lo_s, 3 * CT if t >= 4 else 2 * CT)
                if t >= 2:
                    pe.wait_ge(x2_s, t - 1)
                else:
                    pe.wait_ge(rs_pre, 2)
                r = slice(t * P, (t + 1) * P)
                for half in range(2):
                    w = slice(half * 512, (half + 1) * 512)
                    for k in range(2 * CT):
                        o_ = p_o[t % 2][:, w]
                        pe.matmul(o_, mix_hi[:, k, r], m.wo_hi[:, k, w], start=k == 0, stop=False)
                        pe.matmul(o_, mix_hi[:, k, r], m.wo_lo[:, k, w], start=False, stop=False)
                        ins = pe.matmul(o_, mix_lo[:, k, r], m.wo_hi[:, k, w], start=False, stop=k == 2 * CT - 1)
                ins.then_inc(out_mm, 1)

            def turn(t):
                pe.wait_ge(h2_s, t + 1)
                if t:
                    pe.wait_ge(h2t_s, 2 * t)
                else:
                    pe.wait_ge(mix_lo_s, 3 * CT)
                for k in range(KT):
                    ins = pe.transpose(p_m[k // 4][:, (k % 4) * P:(k % 4 + 1) * P], h2[t % 2][:, k * P:(k + 1) * P],
                                       m.ident[:])
                ins.then_inc(h2_mm, 1)

            def route(t):
                pe.wait_ge(h2t_s, 2 * t + 2)
                if t:
                    pe.wait_ge(log_s, t)
                else:
                    pe.wait_ge(in_s, 48)
                for k in range(KT):
                    ins = pe.matmul(p_l[:], h2t[t % 2][:, k, :], w_router[:, k, :], start=k == 0, stop=k == KT - 1)
                ins.then_inc(log_mm, 1)

            for t in range(T):
                project(t)
                if t:
                    turn(t - 1)
                if t >= 2:
                    route(t - 2)
            turn(T - 1)
            route(T - 2)
            route(T - 1)


def stage_d(nc, m, a):
    NI = ITEMS + 1
    SLOTB = NB * NI
    FAR = 8193
    TK = T * TOPK
    with ExitStack() as ctx:
        place = [0]

        def at(name, shape, dt):
            n = 4
            for s_ in shape[1:]:
                n *= s_
            off = place[0]
            place[0] += -(-n // 64) * 64
            assert place[0] <= 186 * KIB
            return nc.alloc_sbuf_tensor_at("D_" + name, shape, dt, offset=m.base + off)

        def sem(name):
            return ctx.enter_context(nc.semaphore("D_" + name))

        top8, idx8 = at("top8", [P, T, 8], F32), at("idx8", [P, T, 8], U32)
        idx_f, ex, esum = at("idx_f", [P, TK], F32), at("ex", [P, T, TOPK], F32), at("esum", [P, T], F32)
        iota_e, iota_lo, iota_hi = at("iota_e", [P, E_], F32), at("iota_lo", [P, P], F32), at("iota_hi", [P, SLOTB], F32)
        row_no = at("row_no", [P, TK], F32)
        picked = at("picked", [P, TK, E_], F32)
        chosen, chosen_b = at("chosen", [P, T, E_], F32), at("chosen_b", [P, T, E_], BF16)
        tri, ones_b = at("tri", [P, P], BF16), at("ones_b", [P, P], BF16)
        cnt, nch, part, end, first = (at(n, [P, E_], F32) for n in ("cnt", "nch", "part", "end", "first"))
        place_in, slot_of = at("place_in", [P, T, E_], F32), at("slot_of", [P, TK, E_], F32)
        dest, dest_i, lo_i, hi_i = at("dest", [P, TK], F32), at("dest_i", [P, TK], I32), at("lo_i", [P, TK], I32), at("hi_i", [P, TK], I32)
        lo_f, hi_f = at("lo_f", [P, TK], F32), at("hi_f", [P, TK], F32)
        one_lo, val_hi = at("one_lo", [P, TK, P], F32), at("val_hi", [P, TK, 2, SLOTB], F32)
        raw, far, ids_i, ids_f = at("raw", [P, SLOTB], F32), at("far", [P, SLOTB], F32), at("ids_i", [P, SLOTB], I32), at("ids_f", [P, SLOTB], F32)
        iota_i, cmp_, eid, rem, z = at("iota_i", [1, NI], F32), at("cmp", [1, NI, E_], F32), at("eid", [1, NI], F32), at("rem", [1, NI], F32), at("z", [1, E_], F32)
        bgu_rows, bd_rows = at("bgu_rows", [E_, 2 * D], F32), at("bd_rows", [E_, D], F32)

        p_pos = ctx.enter_context(nc.psum_tensor("D_p_pos", [P, T, E_], F32))
        p_cnt = ctx.enter_context(nc.psum_tensor("D_p_cnt", [P, E_], F32))
        p_tab = ctx.enter_context(nc.psum_tensor("D_p_tab", [P, 2, SLOTB], F32))
        p_b = ctx.enter_context(nc.psum_tensor("D_p_b", [P, 32, E_], F32))

        dve_step, pool_step = sem("dve_step"), sem("pool_step")
        consts, gap_s, ex_s, chosen_s, pos_mm, lo_s, tab_mm = (sem(n) for n in (
            "consts", "gap_s", "ex_s", "chosen_s", "pos_mm", "lo_s", "tab_mm"))
        bias_in, bias_mm, bias_s = sem("bias_in"), sem("bias_mm"), sem("bias_s")

        block = ctx.enter_context(nc.Block())

        @block.sync
        def _(sp):
            sp.dma_start(bgu_rows[:], a.b_gate_up[0]).then_inc(bias_in, 16)
            sp.dma_start(bd_rows[:], a.b_down[0]).then_inc(bias_in, 16)

        @block.gpsimd
        def _(pool):
            step = Chain(pool, pool_step)
            for ap, pattern, base, mult in ((iota_e, [[1, E_]], 0, 0), (iota_lo, [[1, P]], 0, 0),
                                            (iota_hi, [[1, SLOTB]], 0, 0), (row_no, [[P, T], [S, TOPK]], 1, 1),
                                            (iota_i, [[1, NI]], 0, 0)):
                step(pool.iota(ap[:], pattern=pattern, base=base, channel_multiplier=mult,
                               allow_small_or_imprecise_dtypes=True))
            step(pool.memset(ones_b[:], 1.0))
            step(pool.affine_select(out=tri[:], in_=ones_b[:], compare_op=ALU.is_gt, fill=0.0, base=0,
                                    pattern=[[1, P]], channel_multiplier=-1))
            pool.memset(z[:], 0.0).then_inc(consts, 1)

        @block.scalar
        def _(act):
            act.wait_ge(gap_s, 1)
            act.activation(ex[:], ex[:], ACT.Exp).then_inc(ex_s, 1)
            act.wait_ge(bias_mm, 1)
            act.activation(m.bias[:], p_b[:, 0:24, :].rearrange("p j e -> p e j"), ACT.Copy).then_inc(bias_s, 1)

        @block.vector
        def _(dve):
            step = Chain(dve, dve_step)
            for t in range(T):
                step(dve.max(top8[:, t, :], m.logits[:, t, :]))
                step(dve.max_index(idx8[:, t, :], top8[:, t, :], m.logits[:, t, :]))
            dve.tensor_tensor(ex[:], top8[:, :, 0:TOPK], top8[:, :, 0:1].to_broadcast([P, T, TOPK]),
                              ALU.subtract).then_inc(gap_s, 1)
            step(dve.tensor_copy(idx_f[:].rearrange("p (t k) -> p t k", k=TOPK), idx8[:, :, 0:TOPK]))
            dve.wait_ge(consts, 1)
            step(dve.tensor_tensor(picked[:], iota_e[:].unsqueeze(1).to_broadcast([P, TK, E_]),
                                   idx_f[:].unsqueeze(2).to_broadcast([P, TK, E_]), ALU.is_equal))
            step(dve.tensor_reduce(chosen[:], picked[:].rearrange("p (t k) e -> p t e k", k=TOPK), AX.X, ALU.add))
            dve.tensor_copy(chosen_b[:], chosen[:]).then_inc(chosen_s, 1)
            dve.wait_ge(ex_s, 1)
            step(dve.tensor_reduce(esum[:], ex[:], AX.X, ALU.add))
            step(dve.reciprocal(esum[:], esum[:]))
            step(dve.tensor_tensor(ex[:], ex[:], esum[:].unsqueeze(2).to_broadcast([P, T, TOPK]), ALU.mult))
            dve.wait_ge(pos_mm, 2)
            step(dve.tensor_copy(cnt[:], p_cnt[:]))
            step(dve.tensor_scalar(nch[:], cnt[:], 0.0, None, ALU.is_gt))
            for q in range(1, S // CHUNK):
                step(dve.tensor_scalar(part[:], cnt[:], float(q * CHUNK), None, ALU.is_gt))
                step(dve.tensor_tensor(nch[:], nch[:], part[:], ALU.add))
            step(dve.memset(part[:], 1.0))
            step(dve.tensor_tensor_scan(out=end[:], data0=part[:], data1=nch[:], initial=0.0, op0=ALU.mult, op1=ALU.add))
            step(dve.tensor_tensor(first[:], end[:], nch[:], ALU.subtract))
            step(dve.tensor_scalar(first[:], first[:], float(CHUNK), None, ALU.mult))
            step(dve.tensor_tensor(place_in[:], p_pos[:], first[:].unsqueeze(1).to_broadcast([P, T, E_]), ALU.add))
            step(dve.tensor_tensor(slot_of[:].rearrange("p (t k) e -> p t k e", k=TOPK),
                                   picked[:].rearrange("p (t k) e -> p t k e", k=TOPK),
                                   place_in[:].unsqueeze(2).to_broadcast([P, T, TOPK, E_]), ALU.mult))
            step(dve.tensor_reduce(dest[:], slot_of[:], AX.X, ALU.add))
            step(dve.tensor_copy(dest_i[:], dest[:]))
            step(dve.tensor_scalar(lo_i[:], dest_i[:], P - 1, None, ALU.bitwise_and))
            step(dve.tensor_scalar(hi_i[:], dest_i[:], 7, None, ALU.logical_shift_right))
            step(dve.tensor_copy(lo_f[:], lo_i[:]))
            step(dve.tensor_copy(hi_f[:], hi_i[:]))
            ex_q = ex[:].rearrange("p t k -> p (t k)")
            for q in range(TK):
                dve.tensor_scalar(one_lo[:, q, :], iota_lo[:], lo_f[:, q:q + 1], None, ALU.is_equal)
                dve.tensor_scalar(val_hi[:, q, 0, :], iota_hi[:], hi_f[:, q:q + 1], row_no[:, q:q + 1],
                                  ALU.is_equal, ALU.mult)
                dve.tensor_scalar(val_hi[:, q, 1, :], iota_hi[:], hi_f[:, q:q + 1], ex_q[:, q:q + 1],
                                  ALU.is_equal, ALU.mult).then_inc(lo_s, 1)
            step(dve.tensor_tensor(cmp_[:], end[0:1, :].unsqueeze(1).to_broadcast([1, NI, E_]),
                                   iota_i[:].unsqueeze(2).to_broadcast([1, NI, E_]), ALU.is_le))
            step(dve.tensor_reduce(eid[:], cmp_[:], AX.X, ALU.add))
            step(dve.tensor_scalar(eid[:], eid[:], float(E_ - 1), None, ALU.min))
            step(dve.tensor_tensor(cmp_[:], iota_e[0:1, :].unsqueeze(1).to_broadcast([1, NI, E_]),
                                   eid[:].unsqueeze(2).to_broadcast([1, NI, E_]), ALU.is_equal))
            step(dve.tensor_tensor(z[:], cnt[0:1, :], first[0:1, :], ALU.add))
            step(dve.tensor_tensor(cmp_[:], cmp_[:], z[:].unsqueeze(1).to_broadcast([1, NI, E_]), ALU.mult))
            step(dve.tensor_reduce(rem[:], cmp_[:], AX.X, ALU.add))
            step(dve.scalar_tensor_tensor(out=rem[:], in0=iota_i[:], scalar=-float(CHUNK), in1=rem[:],
                                          op0=ALU.mult, op1=ALU.add))
            step(dve.tensor_scalar(rem[:], rem[:], float(CHUNK), 0.0, ALU.min, ALU.max))
            step(dve.tensor_copy(m.items[:, :, 0], eid[:]))
            step(dve.tensor_copy(m.items[:, :, 1], rem[:]))
            step(dve.tensor_copy(m.n_items[:], end[0:1, E_ - 1:E_]))
            dve.wait_ge(tab_mm, 1)
            step(dve.tensor_copy(m.gates[:], p_tab[:, 1, :]))
            step(dve.tensor_copy(raw[:], p_tab[:, 0, :]))
            step(dve.tensor_scalar(far[:], raw[:], 0.0, float(FAR), ALU.is_equal, ALU.mult))
            step(dve.scalar_tensor_tensor(out=ids_f[:], in0=raw[:], scalar=-1.0, in1=far[:], op0=ALU.add, op1=ALU.add))
            step(dve.tensor_copy(m.rows_out[:], ids_f[:]))
            step(dve.tensor_copy(ids_i[:], ids_f[:]))
            step(dve.tensor_scalar(ids_i[:], ids_i[:], S - 1, None, ALU.bitwise_and))
            step(dve.tensor_copy(ids_f[:], ids_i[:]))
            step(dve.tensor_tensor(ids_f[:], ids_f[:], far[:], ALU.add))
            step(dve.tensor_copy(m.rows_in[:], ids_f[:]))

        @block.tensor
        def _(pe):
            pe.wait_ge(bias_in, 32)
            for j in range(24):
                src = bgu_rows[:, j * P:(j + 1) * P] if j < 16 else bd_rows[:, (j - 16) * P:(j - 15) * P]
                ins = pe.transpose(p_b[:, j, :], src, m.ident[0:E_, 0:E_])
            ins.then_inc(bias_mm, 1)
            pe.wait_ge(consts, 1)
            pe.wait_ge(chosen_s, 1)
            for t in range(T):
                ins = pe.matmul(p_pos[:, t, :], tri[:], chosen_b[:, t, :], start=True, stop=t == 0)
                for s_ in range(t):
                    ins = pe.matmul(p_pos[:, t, :], ones_b[:], chosen_b[:, s_, :], start=False, stop=s_ == t - 1)
            ins.then_inc(pos_mm, 1)
            for t in range(T):
                ins = pe.matmul(p_cnt[:], ones_b[:], chosen_b[:, t, :], start=t == 0, stop=t == T - 1)
            ins.then_inc(pos_mm, 1)
            for q in range(TK):
                pe.wait_ge(lo_s, q + 1)
                ins = pe.matmul(p_tab[:].rearrange("p a b -> p (a b)"), one_lo[:, q, :],
                                val_hi[:, q, :, :].rearrange("p a b -> p (a b)"), start=q == 0, stop=q == TK - 1)
            ins.then_inc(tab_mm, 1)


WIDTHS = (128, 160, 192, 256)


def stage_e(nc, m, a):
    NC = 12
    CW = 256
    ST, RI = 6, 4
    NP = 4
    with ExitStack() as ctx:
        def at(name, shape, dt, off):
            return nc.alloc_sbuf_tensor_at("E_" + name, shape, dt, offset=m.base + off)

        def sem(name):
            return ctx.enter_context(nc.semaphore("E_" + name))

        w_st = [at(f"w_st{i}", [P, KT, CW], F32, 8 * KIB * i) for i in range(ST)]
        w_hi = [at(f"w_hi{i}", [P, KT, CW], F32R, (48 + 8 * i) * KIB) for i in range(RI)]
        w_lo = [at(f"w_lo{i}", [P, KT, CW], F32R, (80 + 8 * i) * KIB) for i in range(RI)]
        x_hi, x_lo = (at(n, [P, KT, CHUNK], F32R, (112 + 8 * i) * KIB) for i, n in enumerate(("x_hi", "x_lo")))
        a_hi, a_lo = (at(n, [P, KT, CHUNK], F32R, (128 + 8 * i) * KIB) for i, n in enumerate(("a_hi", "a_lo")))
        rows = at("rows", [P, NB, D], F32, 144 * KIB)
        y_t = at("y_t", [P, KT, CHUNK], F32, 152 * KIB)
        y_rows = at("y_rows", [P, NB, D], F32, 160 * KIB)
        gate, sig, up = ([at(f"{n}{i}", [P, 2, CHUNK], F32, (168 + 4 * q + 2 * i) * KIB) for i in range(2)]
                         for q, n in enumerate(("gate", "sig", "up")))
        bias = at("bias", [P, 24], F32, 180 * KIB)
        gates = at("gates", [P, NB], F32, 180 * KIB + 128)
        idx_in = at("idx_in", [P, NB], U32, 180 * KIB + 192)
        idx_out = at("idx_out", [P, NB], U32, 180 * KIB + 256)

        p_g, p_u, p_d, p_t = ([ctx.enter_context(nc.psum_tensor(f"E_{n}{i}", [P, 2, 256], F32)) for i in range(2)]
                              for n in ("p_g", "p_u", "p_d", "p_t"))

        w_in = [sem(f"w_in{i}") for i in range(ST)]
        hi_s, lo_s, chunk_mm = sem("hi_s"), sem("lo_s"), sem("chunk_mm")
        gate_s, up_s, yt_s, y_rows_s = sem("gate_s"), sem("up_s"), sem("yt_s"), sem("y_rows_s")
        FREE = 2
        sig_s, clip_s, prod_s, act_s = sem("sig_s"), sem("clip_s"), sem("prod_s"), sem("act_s")
        a_hi_s, a_lo_s = sem("a_hi_s"), sem("a_lo_s")
        x_mm, x_hi_s, x_lo_s, y_mm = sem("x_mm"), sem("x_hi_s"), sem("x_lo_s"), sem("y_mm")
        gathered, scattered = sem("gathered"), sem("scattered")
        bias_s, gates_s, idx_s = sem("bias_s"), sem("gates_s"), sem("idx_s")
        cleared, gone_s = sem("cleared"), sem("gone_s")

        def by_width(eng, n, body):
            def pick(ws):
                if len(ws) == 1:
                    body(ws[0])
                    return
                with eng.If(n <= ws[0]):
                    body(ws[0])
                with eng.Else():
                    pick(ws[1:])
            pick(WIDTHS)

        def item(eng, i, field, hi):
            return eng.value_load(m.items[0:1, bass.ds(i, 1), field], min_val=0, max_val=hi)

        def count(eng):
            return eng.value_load(m.n_items[0:1, 0:1], min_val=1, max_val=ITEMS - 1)

        block = ctx.enter_context(nc.Block())

        @block.sync
        def _(sp):
            def load(e, c):
                if c < 8:
                    j, up_half = c // 2, c % 2
                    src = a.w_gate_up[0][bass.ds(e, 1), :, up_half * D + j * CW:up_half * D + (j + 1) * CW]
                else:
                    src = a.w_down[0][bass.ds(e, 1), :, (c - 8) * CW:(c - 7) * CW]
                sp.dma_start(w_st[c % ST][:], src.rearrange("o (k p) n -> p (o k) n", p=P)).then_inc(w_in[c % ST], 16)

            n_items = count(sp)
            e0 = item(sp, 0, 0, E_ - 1)
            for c in range(ST):
                load(e0, c)
            with sp.Fori(0, n_items) as i:
                e = item(sp, i, 0, E_ - 1)
                e_next = item(sp, i + 1, 0, E_ - 1)
                for c in range(NC):
                    sp.wait_ge(lo_s, NC * i + c + 1)
                    load(e if c + ST < NC else e_next, (c + ST) % NC)
            for s_ in range(ST):
                sp.wait_ge(w_in[s_], 16 * (2 * n_items + 1))
            sp.sem_inc(gone_s, 1)

        @block.gpsimd
        def _(pool):
            pool.memset(rows[:], 0.0).then_inc(cleared, 1)
            pool.wait_ge(cleared, 1)
            pool.memset(y_rows[:], 0.0).then_inc(cleared, 1)
            pool.wait_ge(cleared, 2)
            for s_ in (gate_s, up_s, yt_s, y_rows_s):
                pool.memset(y_t[:], 0.0).then_inc(s_, FREE)
                pool.wait_ge(s_, FREE)

            def gather(i, k):
                pool.tensor_copy(idx_in[:], m.rows_in[:, bass.ds(i * NB, NB)]).then_inc(idx_s, 1)
                pool.wait_ge(idx_s, k)
                pool.sem_inc(gone_s, 1)
                for b in range(NB):
                    pool.indirect_dma_start(rows[:, b, :], None, m.h2_d, bass.IndirectOffsetOnAxis(ap=idx_in[:, b:b + 1], axis=0),
                                            bounds_check=token_max, oob_is_err=False).then_inc(gathered, 16)

            n_items = count(pool)
            token_max, row_max = pool.to_reg(S - 1), pool.to_reg(TOPK * S - 1)
            gather(0, 1)
            pool.wait_ge(x_mm, NP)
            pool.wait_ge(gathered, 16 * NB)
            gather(1, 2)
            with pool.Fori(0, n_items) as i:
                n = item(pool, i, 1, CHUNK)

                def products(w):
                    for j in range(NP):
                        pool.wait_ge(sig_s, NP * i + j + 1)
                        pool.tensor_tensor(sig[j % 2][:, :, 0:w], gate[j % 2][:, :, 0:w], sig[j % 2][:, :, 0:w],
                                           ALU.mult).then_inc(prod_s, 1)
                        pool.wait_ge(prod_s, NP * i + j + 1)
                        pool.wait_ge(clip_s, NP * i + j + 1)
                        pool.tensor_tensor(up[j % 2][:, :, 0:w], up[j % 2][:, :, 0:w], sig[j % 2][:, :, 0:w],
                                           ALU.mult).then_inc(act_s, 1)

                by_width(pool, n, products)
                pool.wait_ge(x_mm, NP * (i + 2))
                pool.wait_ge(gathered, 16 * NB * (i + 2))
                gather(i + 2, 2 * i + 3)
                pool.wait_ge(scattered, 16 * NB * i)
                pool.tensor_copy(idx_out[:], m.rows_out[:, bass.ds(i * NB, NB)]).then_inc(idx_s, 1)
                pool.wait_ge(idx_s, 2 * i + 4)
                pool.wait_ge(y_rows_s, FREE + NP * (i + 1))
                pool.sem_inc(gone_s, 1)
                for b in range(NB):
                    pool.indirect_dma_start(m.expert_d, bass.IndirectOffsetOnAxis(ap=idx_out[:, b:b + 1], axis=0),
                                            y_rows[:, b, :], None, bounds_check=row_max,
                                            oob_is_err=False).then_inc(scattered, 16)
            pool.wait_ge(gathered, 16 * NB * (n_items + 2))
            pool.wait_ge(scattered, 16 * NB * n_items)
            pool.sem_inc(gone_s, 1)

        @block.scalar
        def _(act):
            def split_hi(c):
                act.activation(w_hi[c % RI][:], w_st[c % ST][:], ACT.Copy).then_inc(hi_s, 1)

            def x_part(i, g):
                act.wait_ge(x_mm, NP * i + g + 1)
                act.activation(x_hi[:, 4 * (g % 2):4 * (g % 2) + 4, (g // 2) * P:(g // 2 + 1) * P],
                               p_t[g % 2][:].rearrange("p a (b n) -> p (a b) n", n=P), ACT.Copy).then_inc(x_hi_s, 1)

            n_items = count(act)
            for c in range(RI):
                act.wait_ge(w_in[c], 16)
                split_hi(c)
            for g in range(NP):
                x_part(0, g)
            with act.Fori(0, n_items) as i:
                n = item(act, i, 1, CHUNK)
                act.wait_ge(y_rows_s, FREE + NP * i)
                act.activation(gates[:], m.gates[:, bass.ds(i * NB, NB)], ACT.Copy).then_inc(gates_s, 1)

                def body(w):
                    def sigmoid(j):
                        act.wait_ge(gate_s, FREE + NP * i + j + 1)
                        act.activation(sig[j % 2][:, :, 0:w], gate[j % 2][:, :, 0:w], ACT.Sigmoid, scale=ALPHA
                                       ).then_inc(sig_s, 1)

                    def act_hi(j):
                        act.wait_ge(act_s, NP * i + j + 1)
                        act.activation(a_hi[:, 2 * j:2 * j + 2, 0:w], up[j % 2][:, :, 0:w], ACT.Copy).then_inc(a_hi_s, 1)

                    def y_part(j):
                        act.wait_ge(y_mm, NP * i + j + 1)
                        if j == 0:
                            act.wait_ge(scattered, 16 * NB * i)
                            act.wait_ge(gates_s, i + 1)
                        nb = -(-w // P)
                        for b in range(nb):
                            ins = act.activation(y_rows[:, b, j * CW:(j + 1) * CW], p_t[j % 2][:, b, :], ACT.Copy,
                                                 scale=gates[:, b:b + 1])
                        ins.then_inc(y_rows_s, 1)

                    for c in range(NC):
                        cc = c + RI
                        if c in (1, 3, 5, 7):
                            sigmoid(c // 2)
                        if c == 7:
                            act_hi(3)
                        act.wait_ge(chunk_mm, NC * i + c + 1)
                        act.wait_ge(w_in[cc % ST], 16 * (2 * i + cc // ST + 1))
                        split_hi(cc)
                        if c in (1, 3, 5):
                            act_hi(c // 2)
                        if c == 7:
                            x_part(i + 1, 0)
                            x_part(i + 1, 1)
                        if c == 8:
                            x_part(i + 1, 2)
                            x_part(i + 1, 3)
                        if c >= 10:
                            y_part(c - 10)
                    y_part(2)
                    y_part(3)

                by_width(act, n, body)

        @block.vector
        def _(dve):
            def split_lo(k, c):
                dve.wait_ge(hi_s, k)
                dve.tensor_tensor(w_lo[c % RI][:], w_st[c % ST][:], f32(w_hi[c % RI][:]), ALU.subtract).then_inc(lo_s, 1)

            def x_part(i, g):
                dve.wait_ge(x_hi_s, NP * i + g + 1)
                r = (slice(None), slice(4 * (g % 2), 4 * (g % 2) + 4), slice((g // 2) * P, (g // 2 + 1) * P))
                dve.tensor_tensor(x_lo[r], p_t[g % 2][:].rearrange("p a (b n) -> p (a b) n", n=P), f32(x_hi[r]),
                                  ALU.subtract).then_inc(x_lo_s, 1)

            n_items = count(dve)
            for c in range(RI):
                split_lo(c + 1, c)
            for g in range(NP):
                x_part(0, g)
            with dve.Fori(0, n_items) as i:
                e = item(dve, i, 0, E_ - 1)
                n = item(dve, i, 1, CHUNK)
                dve.wait_ge(yt_s, FREE + NP * i)
                dve.tensor_copy(bias[:], m.bias[:, bass.ds(e, 1), :].rearrange("p o j -> p (o j)")).then_inc(bias_s, 1)

                def body(w):
                    def clip_gate(j):
                        if j == 0:
                            dve.wait_ge(bias_s, i + 1)
                        dve.wait_ge(chunk_mm, NC * i + 2 * j + 1)
                        for h in range(2):
                            ins = dve.tensor_scalar(gate[j % 2][:, h, 0:w], p_g[j % 2][:, h, 0:w],
                                                    bias[:, 2 * j + h:2 * j + h + 1], LIMIT, ALU.add, ALU.min)
                        ins.then_inc(gate_s, 1)

                    def clip_up(j):
                        dve.wait_ge(chunk_mm, NC * i + 2 * j + 2)
                        for h in range(2):
                            ins = dve.tensor_scalar(up[j % 2][:, h, 0:w], p_u[j % 2][:, h, 0:w],
                                                    bias[:, 8 + 2 * j + h:9 + 2 * j + h], LIMIT, ALU.add, ALU.min)
                        ins.then_inc(up_s, 1)
                        dve.wait_ge(up_s, FREE + NP * i + j + 1)
                        dve.tensor_scalar(up[j % 2][:, :, 0:w], up[j % 2][:, :, 0:w], -LIMIT, 1.0, ALU.max, ALU.add
                                          ).then_inc(clip_s, 1)

                    def act_lo(j):
                        dve.wait_ge(a_hi_s, NP * i + j + 1)
                        dve.tensor_tensor(a_lo[:, 2 * j:2 * j + 2, 0:w], up[j % 2][:, :, 0:w],
                                          f32(a_hi[:, 2 * j:2 * j + 2, 0:w]), ALU.subtract).then_inc(a_lo_s, 1)

                    def y_part(j):
                        dve.wait_ge(chunk_mm, NC * i + 8 + j + 1)
                        for h in range(2):
                            ins = dve.tensor_scalar(y_t[:, 2 * j + h, 0:w], p_d[j % 2][:, h, 0:w],
                                                    bias[:, 16 + 2 * j + h:17 + 2 * j + h], None, ALU.add)
                        ins.then_inc(yt_s, 1)

                    for c in range(NC):
                        if c < 8 and c % 2 == 0:
                            clip_gate(c // 2)
                        if c < 8 and c % 2 == 1:
                            clip_up(c // 2)
                        if c == 7:
                            act_lo(3)
                        if c >= 8:
                            y_part(c - 8)
                        split_lo(NC * i + c + RI + 1, c + RI)
                        if c in (1, 3, 5):
                            act_lo(c // 2)
                        if c == 7:
                            x_part(i + 1, 0)
                            x_part(i + 1, 1)
                        if c == 8:
                            x_part(i + 1, 2)
                            x_part(i + 1, 3)

                by_width(dve, n, body)

        @block.tensor
        def _(pe):
            def turn_rows(i, g, free):
                if g == 0:
                    pe.wait_ge(gathered, 16 * NB * (i + 1))
                free()
                for q in range(4):
                    k = 4 * (g % 2) + q
                    ins = pe.transpose(p_t[g % 2][:, q // 2, (q % 2) * P:(q % 2 + 1) * P],
                                       rows[:, g // 2, k * P:(k + 1) * P], m.ident[:])
                ins.then_inc(x_mm, 1)

            n_items = count(pe)
            for g in range(NP):
                turn_rows(0, g, lambda: pe.wait_ge(x_lo_s, g - 1) if g >= 2 else None)
            with pe.Fori(0, n_items) as i:
                n = item(pe, i, 1, CHUNK)

                def body(w):
                    def chunk(c, banks, xh, xl, k0=0, k1=KT, first=True, last=True):
                        for h in range(2):
                            for k in range(k0, k1):
                                o_ = banks[:, h, 0:w]
                                wh = w_hi[c % RI][:, k, h * P:(h + 1) * P]
                                wl = w_lo[c % RI][:, k, h * P:(h + 1) * P]
                                pe.matmul(o_, wh, xh[:, k, 0:w], start=first and h == 0 and k == 0, stop=False,
                                          skip_group_check=True)
                                pe.matmul(o_, wh, xl[:, k, 0:w], start=False, stop=False, skip_group_check=True)
                                ins = pe.matmul(o_, wl, xh[:, k, 0:w], start=False, stop=k == KT - 1,
                                                skip_group_check=True)
                        if last:
                            ins.then_inc(chunk_mm, 1)

                    def turn_y(j):
                        pe.wait_ge(yt_s, FREE + NP * i + j + 1)
                        if j < 2:
                            pe.wait_ge(x_lo_s, NP * (i + 1) + 3 + j)
                        else:
                            pe.wait_ge(y_rows_s, FREE + NP * i + j - 1)
                        for b in range(-(-w // P)):
                            for h in range(2):
                                ins = pe.transpose(p_t[j % 2][:, b, h * P:(h + 1) * P],
                                                   y_t[:, 2 * j + h, b * P:(b + 1) * P], m.ident[:])
                        ins.then_inc(y_mm, 1)

                    pe.wait_ge(x_lo_s, NP * (i + 1))
                    for c in range(8):
                        j = c // 2
                        pe.wait_ge(lo_s, NC * i + c + 1)
                        pe.wait_ge(gate_s if c % 2 == 0 else up_s, NP * i + j + 1)
                        chunk(c, (p_g if c % 2 == 0 else p_u)[j % 2], x_hi, x_lo)
                    for g in range(2):
                        turn_rows(i + 1, g, lambda: pe.wait_ge(y_rows_s, NP * i + 1 + g))
                    for j in range(4):
                        c = 8 + j
                        pe.wait_ge(lo_s, NC * i + c + 1)
                        pe.wait_ge(yt_s, NP * i + j + 1)
                        if j == 0:
                            pe.wait_ge(a_lo_s, NP * i + 3)
                            chunk(c, p_d[0], a_hi, a_lo, 0, 6, True, False)
                            pe.wait_ge(a_lo_s, NP * i + 4)
                            chunk(c, p_d[0], a_hi, a_lo, 6, KT, False, True)
                            for g in range(2, 4):
                                turn_rows(i + 1, g, lambda: pe.wait_ge(x_lo_s, NP * (i + 1) + g - 1))
                        else:
                            chunk(c, p_d[j % 2], a_hi, a_lo)
                        if j >= 2:
                            turn_y(j - 2)
                    turn_y(2)
                    turn_y(3)

                by_width(pe, n, body)


def stage_f(nc, m, a):
    with ExitStack() as ctx:
        R = 3

        def at(name, shape, dt, off):
            return nc.alloc_sbuf_tensor_at("F_" + name, shape, dt, offset=m.base + off)

        def sem(name):
            return ctx.enter_context(nc.semaphore("F_" + name))

        part = [at(f"part{i}", [P, TOPK + 1, D], F32, 20 * KIB * i) for i in range(R)]
        loaded = [sem(f"loaded{i}") for i in range(R)]
        stored = [sem(f"stored{i}") for i in range(R)]
        step_s, sum_s = sem("step_s"), sem("sum_s")
        block = ctx.enter_context(nc.Block())

        @block.sync
        def _(sp):
            for t in range(T):
                r = slice(t * P, (t + 1) * P)
                if t >= R:
                    sp.wait_ge(stored[t % R], 16 * (t // R))
                sp.dma_start(part[t % R][:, 0:TOPK, :], m.expert_d.rearrange("(k s) d -> s k d", k=TOPK)[r]
                             ).then_inc(loaded[t % R], 16)
                sp.dma_start(part[t % R][:, TOPK, :], m.x2_d[r, :]).then_inc(loaded[t % R], 16)

        @block.scalar
        def _(act):
            for t in range(T):
                act.wait_ge(sum_s, t + 1)
                act.dma_start(a.out[0, t * P:(t + 1) * P, :], part[t % R][:, 0, :]).then_inc(stored[t % R], 16)
            for i in range(R):
                act.wait_ge(stored[i], 16 * len(range(i, T, R)))

        @block.vector
        def _(dve):
            step = Chain(dve, step_s)
            for t in range(T):
                q = part[t % R]
                dve.wait_ge(loaded[t % R], 32 * (t // R + 1))
                step(dve.tensor_tensor(q[:, 0:2, :], q[:, 0:2, :], q[:, 2:4, :], ALU.add))
                step(dve.tensor_tensor(q[:, 0, :], q[:, 0, :], q[:, 1, :], ALU.add))
                dve.tensor_tensor(q[:, 0, :], q[:, 0, :], q[:, 4, :], ALU.add).then_inc(sum_s, 1)


class Memory:
    pass


def build(nc, a, stages="ABCDEF"):
    m = Memory()
    m.base = -(-nc.sbuf_base // 64) * 64

    def at(name, shape, dt, off):
        return nc.alloc_sbuf_tensor_at(name, shape, dt, offset=m.base + off)

    m.qk = at("qk", [P, 2 * CT, S], F32, 64 * KIB)
    m.v = at("v", [P, T, DR], F32, 96 * KIB)
    m.rec = at("rec", [P, CT, S], F32, 112 * KIB)
    m.att = at("att", [P, T, DR], F32, 32 * KIB)
    m.wo_hi = at("wo_hi", [P, KT, D], F32R, 136 * KIB)
    m.wo_lo = at("wo_lo", [P, KT, D], F32R, 168 * KIB)
    o = 204 * KIB
    m.ident = at("ident", [P, P], F32, o)
    m.ident_b = at("ident_b", [P, P], BF16, o + 512)
    m.head_ones = at("head_ones", [P, P], F32, o + 768)
    m.rec_ones = at("rec_ones", [P, P], F32, o + 1280)
    m.mask_b = at("mask_b", [P, P], BF16, o + 1792)
    m.logf = at("logf", [P, T * H], F32, o + 2048)
    m.prm = at("prm", [P, 50], F32, o + 2560)
    m.logits = at("logits", [P, T, E_], F32, 202 * KIB)
    m.x2_d = nc.dram_tensor("x2_rows", (S, D), F32).ap()
    m.expert_d = nc.dram_tensor("expert_rows", (TOPK * S, D), F32).ap()
    m.h2_d = nc.dram_tensor("h2_rows", (S, D), F32).ap()
    NI = ITEMS + 1
    o = 188 * KIB
    m.bias = at("bias", [P, E_, 24], F32, o)
    m.rows_in = at("rows_in", [P, NB * NI], U32, o + 3 * KIB)
    m.rows_out = at("rows_out", [P, NB * NI], U32, o + 3 * KIB + 512)
    m.gates = at("gates", [P, NB * NI], F32, o + 4 * KIB)
    m.items = at("items", [1, NI, 2], I32, o + 4 * KIB + 512)
    m.n_items = at("n_items", [1, 1], I32, o + 5 * KIB)
    o = 204 * KIB
    m.row_sum = at("row_sum", [P, T * H], F32, o + 2304)
    if "A" in stages:
        stage_a(nc, m, a)
    if "B" in stages:
        stage_b(nc, m, a)
    if "C" in stages:
        stage_c(nc, m, a)
    if "D" in stages:
        stage_d(nc, m, a)
    if "E" in stages:
        stage_e(nc, m, a)
    if "F" in stages:
        stage_f(nc, m, a)
    return m


_INS = ["x", "ln1_w", "w_in", "conv_w", "conv_b", "w_rg_a", "b_rg_a", "w_rg_i", "b_rg_i", "rg_lambda", "b_forget",
        "q_norm_w", "k_norm_w", "rec_out_norm_w", "attn_out_norm_w", "w_out", "ln2_w", "w_router", "b_router",
        "w_gate_up", "b_gate_up", "w_down", "b_down"]


def kernel(**inputs):
    import numpy as np
    import concourse.bacc as bacc
    from concourse.bass_utils import run_bass_kernel_spmd

    nc = bacc.Bacc("TRN2", target_bir_lowering=False, num_devices=1)
    arrays, args = {}, Memory()
    for name in _INS:
        v = np.ascontiguousarray(inputs[name])
        arrays[f"in_{name}"] = v
        args.__dict__[name] = nc.dram_tensor(f"in_{name}", v.shape, mybir.dt.from_np(v.dtype), kind="ExternalInput").ap()
    args.out = nc.dram_tensor("out", (1, S, D), F32, kind="ExternalOutput").ap()
    build(nc, args)
    r = run_bass_kernel_spmd(nc, [arrays], core_ids=[0])
    return r.results[0]["out"]
```
